# Optimizing a Trainium2 kernel written in Bass

```python
import jax, jax.numpy as jnp
from jax import lax
import numpy as np

D_MODEL = 2048
BATCH = 1
SEQ = 256
DEPTH = 2

N_MIXERS = 2
N_GLA_LAYERS = (DEPTH + 1) // 2
N_FOX_LAYERS = DEPTH // 2

GLA_HEADS = 4
GLA_KEY_DIM = D_MODEL // 2
GLA_VAL_DIM = D_MODEL
GLA_HEAD_K = GLA_KEY_DIM // GLA_HEADS
GLA_HEAD_V = GLA_VAL_DIM // GLA_HEADS
GLA_GATE_RANK = 16
GLA_GATE_TEMP = 16.0
GLA_CHUNK = 64
GLA_IN = 2 * GLA_KEY_DIM + 2 * GLA_VAL_DIM + GLA_GATE_RANK

FOX_HEAD_DIM = 128
FOX_HEADS = D_MODEL // FOX_HEAD_DIM
FOX_BLOCK = 128
FOX_IN = 4 * D_MODEL + FOX_HEADS

D_FF = ((8 * D_MODEL + 2) // 3 + 255) // 256 * 256

RMS_EPS = 1e-6

kernel_name = "hybrid_gla_fox_interleaved"

def rms_norm(x, g):
    xf = x.astype(jnp.float32)
    y = xf * lax.rsqrt(jnp.mean(xf * xf, axis=-1, keepdims=True) + RMS_EPS)
    return (y * g.astype(jnp.float32)).astype(x.dtype)

def gla_mixer(h, w_in, w_g2, b_g2, o_gain, w_o):
    B, S, _ = h.shape
    H, HK, HV, C = GLA_HEADS, GLA_HEAD_K, GLA_HEAD_V, GLA_CHUNK
    proj = h @ w_in
    q, k, v, r, g_lr = jnp.split(
        proj, [GLA_KEY_DIM, 2 * GLA_KEY_DIM, 2 * GLA_KEY_DIM + GLA_VAL_DIM,
               2 * GLA_KEY_DIM + 2 * GLA_VAL_DIM], axis=-1)
    log_a = jax.nn.log_sigmoid((g_lr @ w_g2 + b_g2).astype(jnp.float32)) / GLA_GATE_TEMP

    def heads(t, dh):
        return t.reshape(B, S, H, dh).transpose(0, 2, 1, 3).astype(jnp.float32)

    q = heads(q, HK) * (HK ** -0.5)
    k = heads(k, HK)
    v = heads(v, HV)
    la = heads(log_a, HK)
    nc = S // C

    def chunks(t):
        return t.reshape(B, H, nc, C, t.shape[-1]).transpose(2, 0, 1, 3, 4)

    qc, kc, vc = chunks(q), chunks(k), chunks(v)
    bc = jnp.cumsum(chunks(la), axis=-2)
    causal = jnp.tril(jnp.ones((C, C), dtype=bool))

    def step(state, inp):
        q_i, k_i, v_i, b_i = inp
        diff = b_i[:, :, :, None, :] - b_i[:, :, None, :, :]
        decay = jnp.exp(jnp.where(causal[:, :, None], diff, -jnp.inf))
        attn = jnp.einsum('bhtk,bhsk,bhtsk->bhts', q_i, k_i, decay)
        o = attn @ v_i + jnp.einsum('bhtk,bhkv->bhtv', q_i * jnp.exp(b_i), state)
        b_last = b_i[:, :, -1:, :]
        state = (jnp.exp(b_last[:, :, 0, :])[..., None] * state
                 + jnp.einsum('bhsk,bhsv->bhkv', k_i * jnp.exp(b_last - b_i), v_i))
        return state, o

    state0 = jnp.zeros((B, H, HK, HV), jnp.float32)
    _, o = lax.scan(step, state0, (qc, kc, vc, bc))
    o = o.transpose(1, 0, 3, 2, 4).reshape(B, S, H, HV)
    o = rms_norm(o, o_gain).reshape(B, S, GLA_VAL_DIM).astype(h.dtype)
    return (o * jax.nn.silu(r)) @ w_o

def fox_mixer(h, w_in, b_f, q_gain, k_gain, w_o):
    B, S, _ = h.shape
    H, HD, BLK = FOX_HEADS, FOX_HEAD_DIM, FOX_BLOCK
    proj = h @ w_in
    q, k, v, f_lr, og = jnp.split(
        proj, [D_MODEL, 2 * D_MODEL, 3 * D_MODEL, 3 * D_MODEL + H], axis=-1)
    q = rms_norm(q.reshape(B, S, H, HD), q_gain).transpose(0, 2, 1, 3)
    k = rms_norm(k.reshape(B, S, H, HD), k_gain).transpose(0, 2, 1, 3)
    v = v.reshape(B, S, H, HD).transpose(0, 2, 1, 3)
    log_f = jax.nn.log_sigmoid((f_lr + b_f).astype(jnp.float32))
    c = jnp.cumsum(log_f.transpose(0, 2, 1), axis=-1)
    scale = HD ** -0.5
    nb = S // BLK
    q_blocks = q.reshape(B, H, nb, BLK, HD).transpose(2, 0, 1, 3, 4)
    cq_blocks = c.reshape(B, H, nb, BLK).transpose(2, 0, 1, 3)
    key_pos = jnp.arange(S)

    def block(args):
        qb, cqb, i = args
        q_pos = i * BLK + jnp.arange(BLK)
        logits = jnp.einsum('bhqd,bhkd->bhqk', qb, k).astype(jnp.float32) * scale
        logits = logits + (cqb[..., None] - c[:, :, None, :])
        logits = jnp.where(key_pos[None, :] <= q_pos[:, None], logits, -jnp.inf)
        p = jax.nn.softmax(logits, axis=-1)
        return jnp.einsum('bhqk,bhkd->bhqd', p.astype(v.dtype), v)

    o = lax.map(block, (q_blocks, cq_blocks, jnp.arange(nb)))
    o = o.transpose(1, 0, 3, 2, 4).reshape(B, S, D_MODEL)
    return (o * jax.nn.sigmoid(og)) @ w_o

def swiglu(h, w_gate, w_up, w_down):
    return (jax.nn.silu(h @ w_gate) * (h @ w_up)) @ w_down

def setup_inputs(seed: int = 0) -> dict:
    key = jax.random.key(seed)
    ks = jax.random.split(key, 17)
    f32 = jnp.float32

    def nrm(k, shape, scale):
        return jax.random.normal(k, shape, f32) * scale

    D = D_MODEL
    return {
        "x": nrm(ks[0], (BATCH, SEQ, D), 1.0),
        "norm_mix": 1.0 + nrm(ks[1], (DEPTH, D), 0.02),
        "norm_ffn": 1.0 + nrm(ks[2], (DEPTH, D), 0.02),
        "gla_w_in": nrm(ks[3], (N_GLA_LAYERS, D, GLA_IN), D ** -0.5),
        "gla_w_g2": nrm(ks[4], (N_GLA_LAYERS, GLA_GATE_RANK, GLA_KEY_DIM), GLA_GATE_RANK ** -0.5),
        "gla_b_g2": nrm(ks[5], (N_GLA_LAYERS, GLA_KEY_DIM), 0.02),
        "gla_o_gain": 1.0 + nrm(ks[6], (N_GLA_LAYERS, GLA_HEAD_V), 0.02),
        "gla_w_o": nrm(ks[7], (N_GLA_LAYERS, GLA_VAL_DIM, D), GLA_VAL_DIM ** -0.5),
        "fox_w_in": nrm(ks[8], (N_FOX_LAYERS, D, FOX_IN), D ** -0.5),
        "fox_b_f": 1.0 + nrm(ks[9], (N_FOX_LAYERS, FOX_HEADS), 0.1),
        "fox_q_gain": 1.0 + nrm(ks[10], (N_FOX_LAYERS, FOX_HEAD_DIM), 0.02),
        "fox_k_gain": 1.0 + nrm(ks[11], (N_FOX_LAYERS, FOX_HEAD_DIM), 0.02),
        "fox_w_o": nrm(ks[12], (N_FOX_LAYERS, D, D), D ** -0.5),
        "ffn_w_gate": nrm(ks[13], (DEPTH, D, D_FF), D ** -0.5),
        "ffn_w_up": nrm(ks[14], (DEPTH, D, D_FF), D ** -0.5),
        "ffn_w_down": nrm(ks[15], (DEPTH, D_FF, D), D_FF ** -0.5),
    }

def reference(x, norm_mix, norm_ffn, gla_w_in, gla_w_g2, gla_b_g2, gla_o_gain, gla_w_o,
              fox_w_in, fox_b_f, fox_q_gain, fox_k_gain, fox_w_o,
              ffn_w_gate, ffn_w_up, ffn_w_down):
    for i in range(DEPTH):
        h = rms_norm(x, norm_mix[i])
        j = i // N_MIXERS
        if i % N_MIXERS == 0:
            mix = gla_mixer(h, gla_w_in[j], gla_w_g2[j], gla_b_g2[j], gla_o_gain[j], gla_w_o[j])
        else:
            mix = fox_mixer(h, fox_w_in[j], fox_b_f[j], fox_q_gain[j], fox_k_gain[j], fox_w_o[j])
        x = x + mix
        h = rms_norm(x, norm_ffn[i])
        x = x + swiglu(h, ffn_w_gate[i], ffn_w_up[i], ffn_w_down[i])
    return x


_drawn_inputs = setup_inputs


def setup_inputs(seed=0):
    import zlib

    import numpy as np

    out = dict(_drawn_inputs(seed))
    spreads = {}
    factors = {'norm_ffn': 3.019,
     'gla_b_g2': 8.0,
     'gla_o_gain': 4.389,
     'fox_b_f': 36.2,
     'fox_q_gain': 32.992,
     'fox_k_gain': 34.592}
    for name, (base, spread) in spreads.items():
        noise = np.random.default_rng([zlib.crc32(name.encode()), seed]).standard_normal(out[name].shape)
        drawn = base * np.exp(spread * noise) if base else spread * noise
        out[name] = __import__('jax').numpy.asarray(drawn.astype(out[name].dtype))
    for name, factor in factors.items():
        out[name] = (out[name] * factor).astype(out[name].dtype)
    return out
```

```python
from contextlib import ExitStack

import numpy as np

import concourse.bass as bass
from concourse import mybir

F32 = mybir.dt.float32
F32R = mybir.dt.float32r
U32 = mybir.dt.uint32
ALU = mybir.AluOpType
ACT = mybir.ActivationFunctionType
AX = mybir.AxisListType

P = 128
SLOTS = 4
KC_CHUNK = 2
N = 512
TB = 2
LEVELS = (64, 32, 16, 8, 4, 2, 1)
NEG = -3.0e38
EPS = 1e-6


class Lin:

    def __init__(self, base, per=0, reg=None):
        self.base, self.per, self.reg = base, per, reg

    def __add__(self, k):
        return Lin(self.base + k, self.per, self.reg)

    def __mul__(self, k):
        return Lin(self.base * k, self.per * k, self.reg)

    def rounds(self):
        assert self.per % SLOTS == 0
        return Lin(self.base // SLOTS, self.per // SLOTS, self.reg)

    @property
    def v(self):
        return self.base if self.reg is None else self.reg * self.per + self.base


def wait(eng, sem, count):
    if count.reg is not None or count.base > 0:
        eng.wait_ge(sem, count.v)


def build(nc, x, norm_mix, norm_ffn, gla_w_in, gla_w_g2, gla_b_g2, gla_o_gain, gla_w_o,
          fox_w_in, fox_b_f, fox_q_gain, fox_k_gain, fox_w_o, w_gate, w_up, w_down, out):
    S, D = x.shape[1], x.shape[2]
    KC = D // P
    DT = D // N
    CH = KC // KC_CHUNK
    DFF = w_gate.shape[2]
    FT = DFF // N
    HC = DFF // P
    HCH = HC // KC_CHUNK
    R = gla_w_g2.shape[1]
    KD = gla_w_g2.shape[2]
    GF = KD // P
    HV = gla_o_gain.shape[1]
    GH = D // HV
    FPH = GF // GH
    HD = fox_q_gain.shape[1]
    FH = D // HD
    QT = KD // N
    assert S == TB * P and HV == N and HD == P and R == FH == 16

    C = {}
    c = 0
    for name, chunks in (("gla_in", (2 * QT + 2 * DT) * CH), ("gla_o", DT * CH), ("ffn0", 2 * FT * CH),
                         ("down0", DT * HCH), ("fox_in", 4 * DT * CH), ("fox_o", DT * CH),
                         ("ffn1", 2 * FT * CH), ("down1", DT * HCH)):
        C[name] = c
        c += chunks
        assert c % SLOTS == 0
    G = {}
    g = 0
    for name, tiles in (("x", DT), ("gla_qk", 2 * QT), ("gla_y", GH), ("gla_o", DT), ("ffn0", FT),
                        ("down0", DT), ("fox_qk", 2 * DT), ("fox_y", DT), ("fox_o", DT), ("ffn1", FT)):
        G[name] = g
        g += tiles
    C_GV = C["gla_in"] + 2 * QT * CH
    C_FV = C["fox_in"] + 2 * DT * CH

    ctx = ExitStack()
    with ctx:
        def sb(name, shape, dt=F32):
            return ctx.enter_context(nc.sbuf_tensor(name, shape, dt))

        def sem(name):
            return ctx.enter_context(nc.semaphore(name))

        xres = sb("xres", [P, TB, D])
        xt_hi = sb("xt_hi", [P, KC, S], F32R)
        xt_lo = sb("xt_lo", [P, KC, S], F32R)
        raw = sb("raw", [P, SLOTS, KC_CHUNK * N])
        w_hi = sb("w_hi", [P, SLOTS, KC_CHUNK * N], F32R)
        w_lo = sb("w_lo", [P, SLOTS, KC_CHUNK * N], F32R)
        stage = sb("stage", [P, TB, N])
        act = sb("act", [P, TB, N])
        ident = sb("ident", [P, P])
        masks = sb("masks", [P, len(LEVELS), P])
        grow = sb("grow", [84, P])
        gcol = sb("gcol", [P, 84])
        b_f = sb("b_f", [FH, 1])
        ones = sb("ones", [P, 2 * P])
        nhalf = sb("nhalf", [P, TB * FH])
        sumsq = sb("sumsq", [P, 4, TB, DT])
        rstd = sb("rstd", [P, 4, TB])
        hsum = sb("hsum", [P, TB * 4])
        hrstd = sb("hrstd", [P, TB * 4])
        psc = sb("psc", [P, 3, TB * 4])
        narrow = sb("narrow", [R, S])
        diag = sb("diag", [P, TB, P])
        ohr = sb("o_rstd", [P, GH, TB])

        base = nc.sbuf_base
        room = [0]

        def at(name, shape, offset, dt=F32):
            size = 4 * int(np.prod(shape[1:]))
            room[0] = max(room[0], offset + size)
            return nc.alloc_sbuf_tensor_at(name, shape, dt, offset=base + offset)
        K = 1024
        ht_hi = at("ht_hi", [P, HC, S], 0, F32R)
        ht_lo = at("ht_lo", [P, HC, S], 44 * K, F32R)
        yt_hi = at("yt_hi", [P, KC, S], 0, F32R)
        yt_lo = at("yt_lo", [P, KC, S], 16 * K, F32R)
        qT = at("gla_qT", [P, GF, S], 0)
        kT = at("gla_kT", [P, GF, S], 8 * K)
        bT = at("gla_bT", [P, GF, S], 16 * K)
        dec = at("gla_dec", [P, GF, S], 24 * K)
        fac = [at(f"gla_fac{i}", [P, GF, S], (32 + 8 * i) * K) for i in range(2)]
        osb = at("gla_o", [P, TB, D], 32 * K)
        a0 = at("gla_a0", [P, GH, S], 48 * K)
        a1 = at("gla_a1", [P, GH, P], 52 * K)
        gv = at("gla_v", [P, TB, D], 54 * K)
        gr = at("gla_silu_r", [P, TB, D], 70 * K)
        wn = at("gla_wn", [P, (KC + 7) * R], 54 * K)
        wn_hi = at("gla_wn_hi", [P, (KC + 7) * R], 56 * K, F32R)
        wn_lo = at("gla_wn_lo", [P, (KC + 7) * R], 58 * K, F32R)
        absz = at("gla_absz", [P, GF, S], 62 * K)
        minz = at("gla_minz", [P, GF, S], 70 * K)
        uu = at("gla_u", [P, GF, S], 78 * K)
        w_g2 = at("gla_w_g2", [R, KD], 86 * K)
        nrT = at("gla_narrow_T", [R, S], 90 * K)
        fqk = at("fox_qkT", [P, 2 * FH, S], 0)
        fv = at("fox_v", [P, TB, D], 32 * K)
        bias = at("fox_bias", [P, FH, S], 48 * K)
        og = at("fox_og", [P, DT, TB, N], 48 * K)
        pT = at("fox_pT", [P, FH, 3 * P], 64 * K)
        prob = at("fox_p", [P, 2, 3 * P], 88 * K)
        fwn = at("fox_wn", [P, (KC + 7) * R], 64 * K)
        fwn_hi = at("fox_wn_hi", [P, (KC + 7) * R], 66 * K, F32R)
        fwn_lo = at("fox_wn_lo", [P, (KC + 7) * R], 68 * K, F32R)
        fz = at("fox_z", [FH, 6, S], 70 * K)
        psums = at("fox_sums", [P, 2, FH], 91 * K)
        prec = at("fox_rec", [P, 2, FH], 91 * K + 128)
        pmax = at("fox_max", [P, 2, 2], 91 * K + 256)
        assert base + room[0] <= nc.sbuf_usable_end, (base, room[0], nc.sbuf_usable_end)
        c_dram = nc.dram_tensor("minus_c", [FH, S], F32, kind="Internal").ap()

        acc = ctx.enter_context(nc.psum_tensor("acc", [P, 2, TB, N], F32))
        tp = ctx.enter_context(nc.psum_tensor("tp", [P, 4, S], F32))
        wk = ctx.enter_context(nc.psum_tensor("wk", [P, 2, N], F32))
        wk4 = wk[:, :, :].rearrange("p b (f t) -> p (b f) t", t=S)

        landed = [sem(f"chunk_landed_{s}") for s in range(SLOTS)]
        hi_done, lo_done, chunk_used = sem("hi_done"), sem("lo_done"), sem("chunk_used")
        x_landed = [sem(f"x_landed_{t}") for t in range(DT)]
        mix_rows_landed, rows_landed, small_landed = sem("norm_mix_landed"), sem("rows_landed"), sem("small_landed")
        narrow_landed = [sem("gla_narrow_landed"), sem("fox_narrow_landed")]
        ident_made, masks_made, consts_made = sem("ident_made"), sem("masks_made"), sem("consts_made")
        pad_made = sem("narrow_pad_made")
        rows_turned, gains_ready = sem("rows_turned"), sem("gains_ready")
        staged, turned, tp_hi, tp_lo = sem("staged"), sem("turned"), sem("tp_hi_read"), sem("tp_lo_read")
        squared, x_saved, rstd_ready = sem("squared"), sem("x_saved"), sem("rstd_ready")
        pool_chain, dve_chain, act_chain = sem("pool_chain"), sem("dve_chain"), sem("act_chain")
        gate_done = sem("gate_done")
        out_stored = sem("out_stored")
        narrow_hi, narrow_lo, narrow_mm, narrow_out = (sem("narrow_hi"), sem("narrow_lo"), sem("narrow_mm"),
                                                       sem("narrow_out"))
        row_done, narrow_T = sem("rstd_row_done"), sem("narrow_T_ready")
        diag_made = sem("rstd_diagonal_made")
        z_mm, z_abs, z_min = sem("z_product"), sem("z_abs"), sem("z_min")
        e_done, u_done, l_done, la_done, b_done = (sem("exp_done"), sem("u_done"), sem("ln_done"),
                                                   sem("log_gate_done"), sem("running_sum_done"))
        d_done, dec_done, fac_done = sem("difference_done"), sem("decay_done"), sem("factors_done")
        a_mm, a_kept, a_zero = sem("level_product"), sem("level_kept"), sem("weights_zeroed")
        v_done, r_done = sem("v_done"), sem("r_done")
        o_mm, o_out, o_sq, o_rstd = sem("o_product"), sem("o_out"), sem("o_squared"), sem("o_rstd")
        raw_qk, head_sq, head_sum, head_rstd = (sem("raw_qk"), sem("head_squares"), sem("head_sums"),
                                                sem("head_rstd"))
        c_ready, c_stored, bias_landed, bias_ready = (sem("minus_c_ready"), sem("minus_c_stored"),
                                                      sem("bias_landed"), sem("bias_ready"))
        qk_mm, prob_done, max_done, prob_turned, pT_done = (sem("logits"), sem("prob_done"), sem("max_done"),
                                                            sem("prob_turned"), sem("prob_T_done"))
        neg_made = sem("causal_mask_made")
        fv_done, og_done, pv_mm, rec_done = sem("fox_v_done"), sem("og_done"), sem("pv_product"), sem("rec_done")

        block = ctx.enter_context(nc.Block())

        GAIN_MIX0, GAIN_MIX1, GAIN_FFN0, GAIN_FFN1, GAIN_O, BIAS_G, GAIN_QK = 0, 16, 32, 48, 64, 68, 76
        ROW_LOADS = 5
        FIRST_TURNS = (0, 1, 4, 6)

        @block.sync
        def _(sp):
            def load(src, row, col, c, j):
                slot = j % SLOTS
                wait(sp, lo_done, c + (j - SLOTS + 1))
                sp.dma_start(
                    raw[:, slot, :].rearrange("p (k n) -> p k n", n=N),
                    src[row:row + KC_CHUNK * P, bass.ds(col, N) if not isinstance(col, int) else slice(col, col + N)]
                    .rearrange("(k p) n -> p k n", p=P)).then_inc(landed[slot], 16)

            def project(src, col0, tiles, c0):
                with sp.Fori(0, tiles // 2) as i:
                    for j in range(2 * CH):
                        load(src, j % CH * KC_CHUNK * P, i * (2 * N) + (col0 + j // CH * N),
                             Lin(c0, 2 * CH, i), j)

            def swiglu(layer, c_up, c_down):
                with sp.Fori(0, FT) as i:
                    for j in range(2 * CH):
                        load((w_gate, w_up)[j // CH][layer], j % CH * KC_CHUNK * P, i * N,
                             Lin(c_up, 2 * CH, i), j)
                with sp.Fori(0, DT // 2) as i:
                    for j in range(2 * HCH):
                        load(w_down[layer], j % HCH * KC_CHUNK * P, i * (2 * N) + j // HCH * N,
                             Lin(c_down, 2 * HCH, i), j)

            for j in range(2 * CH):
                if j < DT:
                    sp.dma_start(xres[:, :, j * N:(j + 1) * N],
                                 x[0, :, j * N:(j + 1) * N].rearrange("(b p) n -> p b n", p=P)) \
                        .then_inc(x_landed[j], 16)
                load(gla_w_in[0], j % CH * KC_CHUNK * P, j // CH * N, Lin(C["gla_in"]), j)
            project(gla_w_in[0], 2 * N, 2 * QT + 2 * DT - 2, C["gla_in"] + 2 * CH)
            project(gla_w_o[0], 0, DT, C["gla_o"])
            swiglu(0, C["ffn0"], C["down0"])
            project(fox_w_in[0], 0, 3 * DT, C["fox_in"])
            project(fox_w_in[0], 3 * D + FH, DT, C["fox_in"] + 3 * DT * CH)
            project(fox_w_o[0], 0, DT, C["fox_o"])
            swiglu(1, C["ffn1"], C["down1"])

        @block.tensor
        def _(pe):
            def turn(n):
                wait(pe, tp_hi, n)
                wait(pe, tp_lo, n)
                src = stage[:, :, :]
                if n.reg is None and n.base < DT:
                    pe.wait_ge(x_landed[n.base], 16)
                    src = xres[:, :, n.base * N:(n.base + 1) * N]
                else:
                    wait(pe, staged, n + (1 - DT))
                for kk in range(N // P):
                    for b in range(TB):
                        last = pe.transpose(tp[:, kk, b * P:(b + 1) * P], src[:, b, kk * P:(kk + 1) * P],
                                            ident[:, :])
                last.then_inc(turned, 1)

            def tile(pair, c, off, hi, lo, chunks=CH, turn_n=None, mid=None, before=None, ready=None):
                for j in range(chunks):
                    if before is not None:
                        before(j)
                    if ready is not None and j == chunks - 2:
                        pe.wait_ge(tp_hi, ready)
                        pe.wait_ge(tp_lo, ready)
                    if j == 4:
                        if turn_n is not None:
                            turn(turn_n)
                        if mid is not None:
                            mid()
                    if j == 6 and turn_n is not None:
                        wait(pe, tp_hi, turn_n + 1)
                        wait(pe, tp_lo, turn_n + 1)
                    slot = (c.base + off + j) % SLOTS
                    wait(pe, lo_done, c + (off + j + 1))
                    for r in range(KC_CHUNK):
                        k = j * KC_CHUNK + r
                        wh = w_hi[:, slot, r * N:(r + 1) * N]
                        wl = w_lo[:, slot, r * N:(r + 1) * N]
                        for b in range(TB):
                            o = acc[:, pair, b, :]
                            xh, xl = hi[:, k, b * P:(b + 1) * P], lo[:, k, b * P:(b + 1) * P]
                            pe.matmul(o, xh, wh, start=(k == 0), stop=False)
                            pe.matmul(o, xh, wl, start=False, stop=False)
                            last = pe.matmul(o, xl, wh, start=False, stop=(k == chunks * KC_CHUNK - 1))
                    last.then_inc(chunk_used, 1)

            def narrow_product(hi, lo, which):
                pe.wait_ge(narrow_lo, which + 1)
                pe.wait_ge(gains_ready, 2)
                for k in range(KC):
                    wh, wl = hi[:, k * R:k * R + P], lo[:, k * R:k * R + P]
                    pe.matmul(wk[:, 0, 0:S], wh, xt_hi[:, k, :], start=(k == 0), stop=False)
                    pe.matmul(wk[:, 0, 0:S], wh, xt_lo[:, k, :], start=False, stop=False)
                    last = pe.matmul(wk[:, 0, 0:S], wl, xt_hi[:, k, :], start=False, stop=(k == KC - 1))
                last.then_inc(narrow_mm, 1)

            def rstd_row(which):
                pe.wait_ge(diag_made, which + 1)
                pe.wait_ge(consts_made, 1)
                for b in range(TB):
                    last = pe.matmul(wk[0:R, 1, b * P:(b + 1) * P], ones[:, 0:R], diag[:, b, :], start=True,
                                     stop=True)
                last.then_inc(row_done, 1)

            def out_and_ffn(c_o, g_o, c_up, g_up, c_down, g_down):
                with pe.Fori(0, DT // 2) as i:
                    for t in range(2):
                        tile(t, Lin(c_o, 2 * CH, i), t * CH, yt_hi, yt_lo, turn_n=Lin(g_o - 1 + t, 2, i))
                with pe.Fori(0, FT) as i:
                    cc = Lin(c_up, 2 * CH, i)
                    tile(0, cc, 0, xt_hi, xt_lo, turn_n=Lin(g_up - 1, 1, i))
                    tile(1, cc, CH, xt_hi, xt_lo)
                if g_down is None:
                    turn(Lin(g_up + FT - 1))
                with pe.Fori(0, DT // 2) as i:
                    for t in range(2):
                        tile(t, Lin(c_down, 2 * HCH, i), t * HCH, ht_hi, ht_lo, HCH,
                             turn_n=None if g_down is None else Lin(g_down - 1 + t, 2, i),
                             ready=g_up + FT if g_down is None else None)

            pe.wait_ge(ident_made, 1)
            turn(Lin(0))
            pe.wait_ge(mix_rows_landed, 16)
            pe.transpose(wk[:, 0, 0:GAIN_FFN0], grow[0:GAIN_FFN0, :], ident[0:GAIN_FFN0, 0:GAIN_FFN0]) \
                .then_inc(rows_turned, 1)
            turn(Lin(1))

            def first_turns(j):
                if j == 3:
                    pe.wait_ge(gains_ready, 1)
                    pe.wait_ge(rows_landed, 16 * ROW_LOADS)
                    pe.transpose(wk[:, 0, 0:84], grow[:, :], ident[0:84, 0:84]).then_inc(rows_turned, 1)
                if j in (2, 4):
                    turn(Lin(j // 2 + 1))
                if j % 2 == 0:
                    pe.wait_ge(tp_hi, j // 2 + 1)
                    pe.wait_ge(tp_lo, j // 2 + 1)
            levels = ["diag", "far"] + list(LEVELS)

            def z_product(half):
                pe.wait_ge(narrow_T, 1)
                pe.wait_ge(small_landed, 32)
                if half == 1:
                    pe.wait_ge(z_abs, 1)
                    pe.wait_ge(z_min, 1)
                for f in range(4):
                    last = pe.matmul(wk4[:, f, :], w_g2[:, (4 * half + f) * P:(4 * half + f + 1) * P],
                                     nrT[:, :], start=True, stop=True)
                last.then_inc(z_mm, 1)

            def level_product(m):
                kind = levels[m]
                if m == 0:
                    pe.wait_ge(tp_hi, G["gla_y"])
                    pe.wait_ge(tp_lo, G["gla_y"])
                    pe.wait_ge(z_abs, 2)
                    pe.wait_ge(z_min, 2)
                else:
                    pe.wait_ge(fac_done, m)
                    pe.wait_ge(a_kept, m)
                f = fac[m % 2]
                for b in range(1 if kind == "far" else TB):
                    for h in range(GH):
                        for kf in range(FPH):
                            ft = FPH * h + kf
                            if kind == "diag":
                                ks, qs = kT[:, ft, b * P:(b + 1) * P], qT[:, ft, b * P:(b + 1) * P]
                            elif kind == "far":
                                ks, qs = f[:, ft, 0:P], f[:, ft, P:S]
                            else:
                                ks = qs = f[:, ft, b * P:(b + 1) * P]
                            last = pe.matmul(wk[:, b, h * P:(h + 1) * P], ks, qs, start=(kf == 0),
                                             stop=(kf == FPH - 1))
                last.then_inc(a_mm, 1)

            def o_product(h):
                pe.wait_ge(a_kept, len(levels))
                pe.wait_ge(v_done, DT)
                if h:
                    pe.wait_ge(o_out, h)
                vh = [gv[:, b, h * HV:(h + 1) * HV] for b in range(TB)]
                pe.matmul(wk[:, 0, :], a0[:, h, 0:P], vh[0], start=True, stop=True)
                pe.matmul(wk[:, 1, :], a0[:, h, P:S], vh[0], start=True, stop=False)
                pe.matmul(wk[:, 1, :], a1[:, h, :], vh[1], start=False, stop=True).then_inc(o_mm, 1)

            gy = G["gla_y"]
            jobs = {(1, 1): lambda: rstd_row(0), (1, 2): lambda: z_product(0), (2, 1): lambda: z_product(1)}
            slots = [(t, s) for t in range(2 * QT, 12) for s in (1, 2)]
            for m in range(len(levels)):
                jobs[slots[2 + m if m else 1]] = lambda m=m: level_product(m)
            first = slots.index((9, 2))
            jobs[slots[first]] = lambda: o_product(0)
            jobs[slots[first + 1]] = lambda: o_product(1)
            jobs[slots[first + 2]] = lambda: (turn(Lin(gy)), o_product(2))
            jobs[slots[first + 3]] = lambda: (turn(Lin(gy + 1)), o_product(3))
            jobs[slots[first + 4]] = lambda: turn(Lin(gy + 2))
            for t in range(2 * QT + 2 * DT):
                tile(t % 2, Lin(C["gla_in"]), t * CH, xt_hi, xt_lo,
                     turn_n=Lin(DT - 1 + t) if 1 <= t <= 2 * QT else None, mid=jobs.get((t, 1)),
                     before=first_turns if t == 0 else None)
                if t == 0:
                    narrow_product(wn_hi, wn_lo, 0)
                if (t, 2) in jobs:
                    jobs[t, 2]()
            out_and_ffn(C["gla_o"], G["gla_o"], C["ffn0"], G["ffn0"], C["down0"], G["down0"])

            with pe.Fori(0, DT) as i:
                for t in range(2):
                    tile(t, Lin(C["fox_in"], 2 * CH, i), t * CH, xt_hi, xt_lo,
                         turn_n=Lin(G["fox_qk"] - 1 + t, 2, i))
            narrow_product(fwn_hi, fwn_lo, 1)

            def logits(h0):
                for h in (h0, h0 + 1):
                    if h >= 2:
                        pe.wait_ge(max_done, h - 1)
                    else:
                        pe.wait_ge(narrow_T, 2)
                        pe.wait_ge(tp_hi, G["fox_y"])
                        pe.wait_ge(tp_lo, G["fox_y"])
                    pe.matmul(wk[:, h % 2, 0:P], fqk[:, h, 0:P], fqk[:, FH + h, 0:P], start=True, stop=True)
                    pe.matmul(wk[:, h % 2, P:3 * P], fqk[:, h, P:S], fqk[:, FH + h, :], start=True,
                              stop=True).then_inc(qk_mm, 1)

            def prob_turn(h0):
                for h in (h0, h0 + 1):
                    pe.wait_ge(prob_done, h + 1)
                    if h >= 2:
                        pe.wait_ge(pT_done, h - 1)
                    o = tp[:, 2 * (h % 2):2 * (h % 2) + 2, :].rearrange("p a t -> p (a t)")
                    for b in range(3):
                        last = pe.transpose(o[:, b * P:(b + 1) * P], prob[:, h % 2, b * P:(b + 1) * P],
                                            ident[:, :])
                    last.then_inc(prob_turned, 1)

            def pv(g):
                pe.wait_ge(pT_done, 4 * g + 4)
                pe.wait_ge(fv_done, DT)
                if g == 0:
                    pe.wait_ge(max_done, FH)
                else:
                    pe.wait_ge(staged, G["fox_y"] + g - DT)
                for hh in range(4):
                    h = 4 * g + hh
                    v0, v1 = fv[:, 0, h * HD:(h + 1) * HD], fv[:, 1, h * HD:(h + 1) * HD]
                    o = [wk[:, b, hh * HD:(hh + 1) * HD] for b in range(TB)]
                    pe.matmul(o[0], pT[:, h, 0:P], v0, start=True, stop=True)
                    pe.matmul(o[1], pT[:, h, P:2 * P], v0, start=True, stop=False)
                    last = pe.matmul(o[1], pT[:, h, 2 * P:3 * P], v1, start=False, stop=True)
                last.then_inc(pv_mm, 1)

            fy = G["fox_y"]
            jobs = {(0, 1): lambda: rstd_row(1)}
            slots = [(t, s) for t in range(2 * DT) for s in (1, 2)]
            first = slots.index((1, 2))
            for h in range(0, FH, 2):
                jobs[slots[first + h // 2]] = lambda h=h: ((prob_turn(h - 2) if h else None), logits(h))
            jobs[slots[first + 8]] = lambda: (prob_turn(FH - 2), pv(0))
            jobs[slots[first + 9]] = lambda: (pe.wait_ge(pT_done, FH), turn(Lin(fy)), pv(1))
            jobs[slots[first + 10]] = lambda: (turn(Lin(fy + 1)), pv(2))
            jobs[slots[first + 11]] = lambda: (turn(Lin(fy + 2)), pv(3))
            for t in range(2 * DT):
                tile(t % 2, Lin(C_FV), t * CH, xt_hi, xt_lo, turn_n=Lin(fy - 1) if t == 0 else None,
                     mid=jobs.get((t, 1)))
                if (t, 2) in jobs:
                    jobs[t, 2]()
            out_and_ffn(C["fox_o"], G["fox_o"], C["ffn1"], G["ffn1"], C["down1"], None)

        @block.scalar
        def _(ac):
            chain = [0]

            def link(ins):
                ins.then_inc(act_chain, 1)
                chain[0] += 1
                ac.wait_ge(act_chain, chain[0])

            def hi(c, j):
                slot = (c.base + j) % SLOTS
                cj = c + j
                wait(ac, landed[slot], cj.rounds() * 16 + 16)
                wait(ac, chunk_used, cj + (1 - SLOTS))
                nc.scalar.activation(w_hi[:, slot, :], raw[:, slot, :], ACT.Copy).then_inc(hi_done, 1)

            def tile(c, off, empty, turned_tile=None, mid=None, chunks=CH):
                for j in range(3):
                    hi(c, off + j)
                if empty is not None:
                    empty()
                for j in range(3, 7):
                    hi(c, off + j)
                if turned_tile is not None:
                    turned_tile()
                if mid is not None:
                    mid()
                if chunks == CH:
                    hi(c, off + 7)
                else:
                    long_tail(c, off)

            def long_tail(c, off):
                hi(c, off + 7)
                with ac.Fori(0, 3) as i:
                    for j in range(SLOTS):
                        hi(Lin(c.base + off + 8, SLOTS, i), j)
                for j in range(20, HCH):
                    hi(c, off + j)

            def squares(n, norm, t):
                src = stage[:, :, :] if n is not None else xres[:, :, t * N:(t + 1) * N]
                if n is not None:
                    ac.wait_ge(staged, n + 1 - DT)
                elif t:
                    ac.wait_ge(squared, t)
                for b in range(TB):
                    last = nc.scalar.activation(act[:, b, :], src[:, b, :], ACT.Square,
                                                accum_out=sumsq[:, norm, b, t:t + 1])
                last.then_inc(squared, 1)

            def turn_x(n, gain, t):
                ac.wait_ge(turned, n + 1)
                for kk in range(4):
                    k = 4 * t + kk
                    last = nc.scalar.activation(xt_hi[:, k, :], tp[:, kk, :], ACT.Copy,
                                                scale=gcol[:, gain + k:gain + k + 1])
                last.then_inc(tp_hi, 1)

            def turn_h(n, t):
                wait(ac, turned, n + 1)
                nc.scalar.activation(ht_hi[:, bass.ds(t.v * 4, 4), :] if t.reg is not None
                                     else ht_hi[:, 4 * t.base:4 * t.base + 4, :],
                                     tp[:, :, :], ACT.Copy).then_inc(tp_hi, 1)

            def turn_y(n, t, gain):
                ac.wait_ge(turned, n + 1)
                if gain is None:
                    nc.scalar.activation(yt_hi[:, 4 * t:4 * t + 4, :], tp[:, :, :], ACT.Copy).then_inc(tp_hi, 1)
                    return
                for kk in range(4):
                    last = nc.scalar.activation(yt_hi[:, 4 * t + kk, :], tp[:, kk, :], ACT.Copy,
                                                scale=gcol[:, gain + kk:gain + kk + 1])
                last.then_inc(tp_hi, 1)

            def scaled(dst, pair, used, norm, func, done, free=None):
                wait(ac, chunk_used, used)
                if free is not None:
                    wait(ac, turned, free)
                for b in range(TB):
                    last = nc.scalar.activation(dst(b), acc[:, pair, b, :], func,
                                                scale=rstd[:, norm, b:b + 1])
                last.then_inc(done, 1)

            def narrow_split(src, hi_, which):
                ac.wait_ge(narrow_landed[which], 16)
                ac.wait_ge(pad_made, 1 + which)
                nc.scalar.activation(hi_[:, :], src[:, :], ACT.Copy).then_inc(narrow_hi, 1)

            def narrow_read(which):
                ac.wait_ge(narrow_mm, which + 1)
                nc.scalar.activation(narrow[:, :], wk[0:R, 0, 0:S], ACT.Copy).then_inc(narrow_out, 1)

            def out_and_ffn(c_o, g_o, c_up, g_up, c_down, g_down, norm, first, first_turn, after):
                gain = (0, GAIN_FFN0, 0, GAIN_FFN1)[norm]
                for t in range(DT):
                    tile(Lin(c_o), t * CH, first if t == 0 else lambda: squares(g_o + t - 1, norm, t - 1),
                         first_turn if t == 0 else lambda: turn_x(g_o + t - 1, gain, t - 1))

                def silu(i):
                    used = Lin(c_up + CH, 2 * CH, i) if i is not None else Lin(c_up + CH)
                    wait(ac, chunk_used, used)
                    wait(ac, staged, Lin(g_up - DT, 1, i) if i is not None else Lin(g_up - DT))
                    if i is None:
                        ac.wait_ge(rstd_ready, norm + 1)
                    for b in range(TB):
                        last = nc.scalar.activation(act[:, b, :], acc[:, 0, b, :], ACT.Silu,
                                                    scale=rstd[:, norm, b:b + 1])
                    last.then_inc(gate_done, 1)
                tile(Lin(c_up), 0, lambda: squares(g_o + 3, norm, 3), lambda: turn_x(g_o + 3, gain, 3))
                tile(Lin(c_up), CH, lambda: silu(None))
                with ac.Fori(1, FT) as i:
                    cc = Lin(c_up, 2 * CH, i)
                    tile(cc, 0, None, lambda: turn_h(Lin(g_up - 1, 1, i), Lin(-1, 1, i)))
                    tile(cc, CH, lambda: silu(i))
                for t in range(DT):
                    if g_down is None and t:
                        tile(Lin(c_down), t * HCH, None, chunks=HCH)
                    elif t == 0:
                        tile(Lin(c_down), 0, None, lambda: turn_h(Lin(g_up + FT - 1), Lin(FT - 1)), chunks=HCH)
                    else:
                        tile(Lin(c_down), t * HCH, lambda: squares(g_down + t - 1, after, t - 1),
                             lambda: turn_x(g_down + t - 1, (GAIN_MIX0, 0, GAIN_MIX1, 0)[after], t - 1), chunks=HCH)

            def load_narrow(dst, src, which):
                ac.dma_start(dst[:, 0:KC * R].rearrange("p (k r) -> p k r", r=R),
                             src.rearrange("(k p) r -> p k r", p=P)).then_inc(narrow_landed[which], 16)

            rows = [(GAIN_MIX0, norm_mix.rearrange("l (k p) -> (l k) p", p=P)),
                    (GAIN_FFN0, norm_ffn.rearrange("l (k p) -> (l k) p", p=P)),
                    (GAIN_O, gla_o_gain[0].rearrange("(k p) -> k p", p=P)),
                    (BIAS_G, gla_b_g2[0].rearrange("(k p) -> k p", p=P)),
                    (GAIN_QK, fox_q_gain.to_broadcast([DT, P])), (GAIN_QK + DT, fox_k_gain.to_broadcast([DT, P]))]
            assert len(rows) == ROW_LOADS + 1
            for r0, src in rows:
                ac.dma_start(grow[r0:r0 + src.shape[0], :], src) \
                    .then_inc(rows_landed if r0 else mix_rows_landed, 16)
            ac.dma_start(w_g2[:, :], gla_w_g2[0]).then_inc(small_landed, 16)
            ac.dma_start(b_f[:, :], fox_b_f.rearrange("a h -> h a")).then_inc(small_landed, 16)
            load_narrow(wn, gla_w_in[0][:, 2 * KD + 2 * D:2 * KD + 2 * D + R], 0)
            ac.wait_ge(gains_ready, 1)

            c0 = Lin(C["gla_in"])
            g0 = G["gla_qk"]

            def gla_qk_turn(n):
                t = n - g0
                dst, s, f = (qT, (KD // GH) ** -0.5, 4 * t) if t < QT else (kT, 1.0, 4 * (t - QT))
                ac.wait_ge(turned, n + 1)
                nc.scalar.activation(dst[:, f:f + 2, :], tp[:, 0:2, :], ACT.Copy, scale=s).then_inc(tp_hi, 1)

            def stage_qk(t):
                scaled(lambda b: stage[:, b, :], t % 2, c0 + (t + 1) * CH, 0, ACT.Copy, staged,
                       free=Lin(g0 + t))

            def z_read(half):
                ac.wait_ge(z_mm, half + 1)
                for f in range(4):
                    ff = 4 * half + f
                    last = nc.scalar.activation(absz[:, ff, :], wk4[:, f, :], ACT.Abs,
                                                bias=gcol[:, BIAS_G + ff:BIAS_G + ff + 1])
                last.then_inc(z_abs, 1)

            def gate_exp():
                ac.wait_ge(z_abs, 2)
                nc.scalar.activation(absz[:, :, :], absz[:, :, :], ACT.Exp, scale=-1.0).then_inc(e_done, 1)

            def gate_ln():
                ac.wait_ge(u_done, 2)
                nc.scalar.activation(dec[:, :, :], uu[:, :, :], ACT.Ln).then_inc(l_done, 1)

            levels = ["far"] + list(LEVELS)

            def decays(m):
                ac.wait_ge(d_done, m)
                if m == 1:
                    nc.scalar.activation(dec[:, :, P:S], bT[:, :, P:S], ACT.Exp, scale=1.0 / 16)
                    nc.scalar.activation(dec[:, :, 0:P], dec[:, :, 0:P], ACT.Exp,
                                         scale=1.0 / 16).then_inc(dec_done, 1)
                else:
                    nc.scalar.activation(dec[:, :, :], dec[:, :, :], ACT.Exp, scale=1.0 / 16).then_inc(dec_done, 1)

            def o_read(h):
                ac.wait_ge(o_mm, h + 1)
                for b in range(TB):
                    nc.scalar.activation(osb[:, b, h * HV:(h + 1) * HV], wk[:, b, :], ACT.Copy)
                if h:
                    ac.wait_ge(o_rstd, h)
                for b in range(TB):
                    last = nc.scalar.activation(act[:, b, :], wk[:, b, :], ACT.Square,
                                                accum_out=hsum[:, b:b + 1])
                last.then_inc(o_out, 1)

            gy = G["gla_y"]
            jobs = {(0, 2): lambda: narrow_read(0), (1, 2): lambda: z_read(0), (2, 1): lambda: z_read(1),
                    (2, 2): gate_exp, (3, 1): gate_ln}
            slots = [(t, s) for t in range(2 * QT, 12) for s in (1, 2)]
            for m in range(1, len(levels) + 1):
                jobs[slots[1 + m]] = lambda m=m: decays(m)
            first = slots.index((9, 2))
            for h in range(GH):
                jobs[slots[first + h]] = (lambda h=h: ((turn_y(gy + h - 2, h - 2, GAIN_O) if h >= 2 else None),
                                                       o_read(h)))
            jobs[slots[first + 4]] = lambda: turn_y(gy + 2, 2, GAIN_O)

            def empty(t):
                if t < 2 * QT:
                    stage_qk(t)
                elif t < 2 * QT + DT:
                    tt = t - 2 * QT
                    if tt == 0:
                        ac.wait_ge(la_done, 1)
                    scaled(lambda b: gv[:, b, tt * N:(tt + 1) * N], t % 2, c0 + (t + 1) * CH, 0, ACT.Copy, v_done)
                else:
                    tt = t - 2 * QT - DT
                    if tt == 0:
                        ac.wait_ge(b_done, 1)
                    scaled(lambda b: gr[:, b, tt * N:(tt + 1) * N], t % 2, c0 + (t + 1) * CH, 0, ACT.Silu, r_done)
                if (t, 2) in jobs:
                    jobs[t, 2]()

            for t in range(2 * QT + 2 * DT):
                if t == 0:
                    for j in range(CH):
                        if j in FIRST_TURNS:
                            n = FIRST_TURNS.index(j)
                            turn_x(n, GAIN_MIX0, n)
                        if j == CH - 1:
                            narrow_split(wn, wn_hi, 0)
                        hi(c0, j)
                    for n in range(DT):
                        squares(None, 0, n)
                else:
                    if t == 1:
                        ac.wait_ge(rstd_ready, 1)
                    tile(c0, t * CH, lambda: empty(t - 1),
                         (lambda: gla_qk_turn(g0 + t - 1)) if t <= 2 * QT else None, jobs.get((t, 1)))
            out_and_ffn(C["gla_o"], G["gla_o"], C["ffn0"], G["ffn0"], C["down0"], G["down0"], 1,
                        lambda: empty(2 * QT + 2 * DT - 1), lambda: turn_y(gy + 3, 3, GAIN_O), 2)

            cf = C["fox_in"]
            gq = G["fox_qk"]

            def stage_raw(t):
                scaled(lambda b: stage[:, b, :], t.base % 2, Lin(cf + (t.base + 1) * CH, t.per * CH, t.reg), 2,
                       ACT.Copy, raw_qk, free=t + gq)

            def fox_turn(t):
                wait(ac, turned, t + (gq + 1))
                if t.reg is None:
                    dst = fqk[:, 4 * t.base:4 * t.base + 2, :]
                    gain = gcol[:, GAIN_QK + t.base:GAIN_QK + t.base + 1]
                else:
                    dst, gain = fqk[:, bass.ds(t.v * 4, 2), :], gcol[:, bass.ds(t.v + GAIN_QK, 1)]
                nc.scalar.activation(dst, tp[:, 0:2, :], ACT.Copy, scale=gain).then_inc(tp_hi, 1)

            tile(Lin(cf), 0, lambda: squares(G["down0"] + 3, 2, 3),
                 lambda: turn_x(G["down0"] + 3, GAIN_MIX1, 3))
            ac.wait_ge(rstd_ready, 3)
            ac.wait_ge(x_saved, 2 * DT)
            ac.wait_ge(chunk_used, C["fox_in"])
            load_narrow(fwn, fox_w_in[0][:, 3 * D:3 * D + FH], 1)
            with ac.Fori(0, DT - 1) as i:
                for t in range(2):
                    tile(Lin(cf + CH, 2 * CH, i), t * CH, lambda: stage_raw(Lin(t, 2, i)),
                         lambda: fox_turn(Lin(t, 2, i)))
            tile(Lin(cf), 7 * CH, lambda: stage_raw(Lin(6)), lambda: fox_turn(Lin(6)))
            narrow_split(fwn, fwn_hi, 1)

            def forget():
                ac.wait_ge(narrow_T, 2)
                link(nc.scalar.activation(fz[:, 1, :], fz[:, 0, :], ACT.Abs))
                link(nc.scalar.activation(fz[:, 2, :], fz[:, 1, :], ACT.Exp, scale=-1.0))
                link(nc.scalar.activation(fz[:, 3, :], fz[:, 2, :], ACT.Copy, bias=1.0))
                nc.scalar.activation(fz[:, 4, :], fz[:, 3, :], ACT.Ln).then_inc(l_done, 1)

            def softmax(h0):
                for h in (h0, h0 + 1):
                    ac.wait_ge(max_done, h + 1)
                    for b in range(TB):
                        s = slice(0, P) if b == 0 else slice(P, 3 * P)
                        last = nc.scalar.activation(prob[:, h % 2, s], prob[:, h % 2, s], ACT.Exp,
                                                    bias=pmax[:, h % 2, b:b + 1], accum_out=psums[:, b, h:h + 1])
                    last.then_inc(prob_done, 1)

            def prob_read(h0):
                for h in (h0, h0 + 1):
                    ac.wait_ge(prob_turned, h + 1)
                    src = tp[:, 2 * (h % 2):2 * (h % 2) + 2, :].rearrange("p a t -> p (a t)")
                    nc.scalar.activation(pT[:, h, :], src[:, 0:3 * P], ACT.Copy).then_inc(pT_done, 1)

            fy = G["fox_y"]
            jobs = {(0, 1): forget}
            slots = [(t, s) for t in range(2 * DT) for s in (1, 2)]
            first = slots.index((1, 2))
            for h in range(0, FH, 2):
                jobs[slots[first + h // 2]] = lambda h=h: ((prob_read(h - 2) if h else None), softmax(h))
            jobs[slots[first + 8]] = lambda: prob_read(FH - 2)
            for g in range(3):
                jobs[slots[first + 9 + g]] = lambda g=g: turn_y(fy + g, g, None)

            def empty1(t):
                if t < DT:
                    scaled(lambda b: fv[:, b, t * N:(t + 1) * N], t % 2, Lin(C_FV + (t + 1) * CH), 2, ACT.Copy, fv_done)
                else:
                    ac.wait_ge(max_done, 4 * (t - DT) + 4)
                    scaled(lambda b: og[:, t - DT, b, :], t % 2, Lin(C_FV + (t + 1) * CH), 2, ACT.Sigmoid, og_done)
                if (t, 2) in jobs:
                    jobs[t, 2]()

            def first_empty():
                stage_raw(Lin(7))
                narrow_read(1)
            tile(Lin(C_FV), 0, first_empty, lambda: fox_turn(Lin(7)), jobs.get((0, 1)))
            for t in range(1, 2 * DT):
                tile(Lin(C_FV), t * CH, lambda: empty1(t - 1), None, jobs.get((t, 1)))
            out_and_ffn(C["fox_o"], G["fox_o"], C["ffn1"], G["ffn1"], C["down1"], None, 3,
                        lambda: empty1(2 * DT - 1), lambda: turn_y(fy + 3, 3, None), None)

        @block.vector
        def _(ve):
            chain = [0]

            def link(ins):
                ins.then_inc(dve_chain, 1)
                chain[0] += 1
                ve.wait_ge(dve_chain, chain[0])

            def lo(c, j):
                slot = (c.base + j) % SLOTS
                wait(ve, hi_done, c + (j + 1))
                nc.vector.tensor_tensor(w_lo[:, slot, :], raw[:, slot, :], w_hi[:, slot, :].bitcast(F32),
                                        ALU.subtract).then_inc(lo_done, 1)

            def tile(c, off, empty=None, turned_tile=None, mid=None, chunks=CH, late=None):
                for j in range(3):
                    lo(c, off + j)
                if empty is not None:
                    empty()
                lo(c, off + 3)
                if late is not None:
                    late()
                for j in range(4, 7):
                    lo(c, off + j)
                if turned_tile is not None:
                    turned_tile()
                if mid is not None:
                    mid()
                lo(c, off + 7)
                if chunks > CH:
                    with ve.Fori(0, 3) as i:
                        for j in range(SLOTS):
                            lo(Lin(c.base + off + 8, SLOTS, i), j)
                    for j in range(20, HCH):
                        lo(c, off + j)

            def add_x(n, m, pair, used, t, saved):
                ve.wait_ge(chunk_used, used)
                ve.wait_ge(turned, n)
                if m is not None:
                    ve.wait_ge(squared, m)
                if saved:
                    ve.wait_ge(x_saved, saved)
                nc.vector.tensor_tensor(stage[:, :, :], acc[:, pair, :, :], xres[:, :, t * N:(t + 1) * N],
                                        ALU.add).then_inc(staged, 1)

            def turn_x(n, gain, t):
                ve.wait_ge(tp_hi, n + 1)
                for kk in range(4):
                    k = 4 * t + kk
                    last = nc.vector.scalar_tensor_tensor(
                        out=xt_lo[:, k, :], in0=tp[:, kk, :], scalar=gcol[:, gain + k:gain + k + 1],
                        in1=xt_hi[:, k, :].bitcast(F32), op0=ALU.mult, op1=ALU.subtract)
                last.then_inc(tp_lo, 1)

            def turn_h(n, t):
                wait(ve, tp_hi, n + 1)
                s = bass.ds(t.v * 4, 4) if t.reg is not None else slice(4 * t.base, 4 * t.base + 4)
                nc.vector.tensor_tensor(ht_lo[:, s, :], tp[:, :, :], ht_hi[:, s, :].bitcast(F32),
                                        ALU.subtract).then_inc(tp_lo, 1)

            def turn_y(n, t, gain):
                ve.wait_ge(tp_hi, n + 1)
                if gain is None:
                    nc.vector.tensor_tensor(yt_lo[:, 4 * t:4 * t + 4, :], tp[:, :, :],
                                            yt_hi[:, 4 * t:4 * t + 4, :].bitcast(F32),
                                            ALU.subtract).then_inc(tp_lo, 1)
                    return
                for kk in range(4):
                    k = 4 * t + kk
                    last = nc.vector.scalar_tensor_tensor(
                        out=yt_lo[:, k, :], in0=tp[:, kk, :], scalar=gcol[:, gain + kk:gain + kk + 1],
                        in1=yt_hi[:, k, :].bitcast(F32), op0=ALU.mult, op1=ALU.subtract)
                last.then_inc(tp_lo, 1)

            def narrow_split(src, hi_, lo_, which):
                ve.wait_ge(narrow_hi, which + 1)
                nc.vector.tensor_tensor(lo_[:, :], src[:, :], hi_[:, :].bitcast(F32),
                                        ALU.subtract).then_inc(narrow_lo, 1)

            def out_and_ffn(c_o, g_o, c_up, g_up, c_down, g_down, m, norm, first, first_turn, saved):
                gain = (0, GAIN_FFN0, 0, GAIN_FFN1)[norm]

                def add_o(t):
                    add_x(g_o + t, m + t if t else None, t % 2, c_o + (t + 1) * CH, t, saved + t)
                for t in range(DT):
                    tile(Lin(c_o), t * CH, first if t == 0 else lambda: add_o(t - 1),
                         first_turn if t == 0 else lambda: turn_x(g_o + t - 1, gain, t - 1))

                def hidden(i):
                    wait(ve, chunk_used, Lin(c_up + (i.base + 1) * 2 * CH, i.per * 2 * CH, i.reg))
                    wait(ve, gate_done, i + ((norm // 2) * FT + 1))
                    wait(ve, turned, i + g_up)
                    if i.reg is None and i.base == 0:
                        ve.wait_ge(squared, m + DT)
                        ve.wait_ge(x_saved, saved + DT)
                        ve.wait_ge(rstd_ready, norm + 1)
                    for b in range(TB):
                        last = nc.vector.scalar_tensor_tensor(
                            out=stage[:, b, :], in0=acc[:, 1, b, :], scalar=rstd[:, norm, b:b + 1],
                            in1=act[:, b, :], op0=ALU.mult, op1=ALU.mult)
                    last.then_inc(staged, 1)

                tile(Lin(c_up), 0, lambda: add_o(3), lambda: turn_x(g_o + 3, gain, 3))
                tile(Lin(c_up), CH)
                tile(Lin(c_up), 2 * CH, lambda: hidden(Lin(0)), lambda: turn_h(Lin(g_up), Lin(0)))
                tile(Lin(c_up), 3 * CH)
                with ve.Fori(2, FT) as i:
                    cc = Lin(c_up, 2 * CH, i)
                    tile(cc, 0, lambda: hidden(Lin(-1, 1, i)), lambda: turn_h(Lin(g_up - 1, 1, i), Lin(-1, 1, i)))
                    tile(cc, CH)
                for t in range(DT):
                    if t == 0:
                        tile(Lin(c_down), 0, lambda: hidden(Lin(FT - 1)),
                             lambda: turn_h(Lin(g_up + FT - 1), Lin(FT - 1)), chunks=HCH)
                    elif g_down is None:
                        tile(Lin(c_down), t * HCH, lambda: last_x(t - 1), chunks=HCH)
                    else:
                        tile(Lin(c_down), t * HCH,
                             lambda: add_x(g_down + t - 1, m + DT + t - 1 if t > 1 else None, (t - 1) % 2,
                                           c_down + t * HCH, t - 1, saved + DT + t - 1),
                             lambda: turn_x(g_down + t - 1, GAIN_MIX1, t - 1), chunks=HCH)

            ve.wait_ge(rows_turned, 1)
            nc.vector.tensor_copy(gcol[:, 0:GAIN_FFN0], wk[:, 0, 0:GAIN_FFN0]).then_inc(gains_ready, 1)
            ve.wait_ge(gains_ready, 1)
            c0 = Lin(C["gla_in"])
            g0 = G["gla_qk"]

            def gla_qk_turn(n):
                t = n - g0
                dst, s, f = (qT, (KD // GH) ** -0.5, 4 * t) if t < QT else (kT, 1.0, 4 * (t - QT))
                ve.wait_ge(turned, n + 1)
                nc.vector.tensor_scalar(dst[:, f + 2:f + 4, :], tp[:, 2:4, :], s, None, ALU.mult).then_inc(tp_lo, 1)

            def rstd_diagonal(norm):
                ve.wait_ge(rstd_ready, norm + 1)
                for b in range(TB):
                    last = nc.vector.tensor_scalar(diag[:, b, :], ident[:, :], rstd[:, norm, b:b + 1], None,
                                                   ALU.mult)
                last.then_inc(diag_made, 1)

            def narrow_T_read():
                ve.wait_ge(row_done, 1)
                ve.wait_ge(narrow_out, 1)
                nc.vector.tensor_tensor(nrT[:, :], narrow[:, :], wk[0:R, 1, 0:S], ALU.mult).then_inc(narrow_T, 1)

            def z_read(half):
                ve.wait_ge(z_mm, half + 1)
                ve.wait_ge(z_abs, half + 1)
                for f in range(4):
                    ff = 4 * half + f
                    last = nc.vector.tensor_scalar(minz[:, ff, :], wk4[:, f, :],
                                                   gcol[:, BIAS_G + ff:BIAS_G + ff + 1], 0.0, ALU.add, ALU.min)
                last.then_inc(z_min, 1)

            def gate_u():
                ve.wait_ge(e_done, 1)
                nc.vector.tensor_scalar(uu[:, :, :], absz[:, :, :], 1.0, None, ALU.add).then_inc(u_done, 1)
                ve.wait_ge(u_done, 1)
                nc.vector.tensor_scalar(bT[:, :, :], uu[:, :, :], 1.0, None, ALU.subtract).then_inc(u_done, 1)

            def running_sums():
                ve.wait_ge(la_done, 1)
                ve.wait_ge(consts_made, 1)
                for f in range(GF):
                    for b in range(TB):
                        s = slice(b * P, (b + 1) * P)
                        last = nc.vector.tensor_tensor_scan(bT[:, f, s], ones[:, 0:P], minz[:, f, s], 0.0,
                                                            ALU.mult, ALU.add)
                last.then_inc(b_done, 1)

            levels = ["far"] + list(LEVELS)

            def factors(m):
                ve.wait_ge(dec_done, m)
                if m > 2:
                    ve.wait_ge(a_mm, m - 1)
                h = P if m == 1 else LEVELS[m - 2]

                def halves(t):
                    return t[:, :, :].rearrange("p f (g two h) -> p (f g) two h", two=2, h=h)
                f, d = halves(fac[m % 2]), halves(dec)
                nc.vector.tensor_tensor(f[:, :, 0, :], halves(kT)[:, :, 0, :], d[:, :, 0, :], ALU.mult)
                nc.vector.tensor_tensor(f[:, :, 1, :], halves(qT)[:, :, 1, :], d[:, :, 1, :],
                                        ALU.mult).then_inc(fac_done, 1)

            def keep(m):
                ve.wait_ge(a_mm, m + 1)
                if m == 0:
                    ve.wait_ge(a_zero, 2)
                    ve.wait_ge(masks_made, 1)
                if m == 1:
                    nc.vector.tensor_copy(a0[:, :, P:S], wk[:, 0, :].rearrange("p (h t) -> p h t", h=GH)) \
                        .then_inc(a_kept, 1)
                    return
                mask = (ident[:, :] if m == 0 else masks[:, m - 2, :]).bitcast(U32)
                mask = mask.unsqueeze(1).to_broadcast([P, GH, P])
                for b in range(TB):
                    dst = a0[:, :, 0:P] if b == 0 else a1[:, :, :]
                    last = nc.vector.copy_predicated(dst, mask, wk[:, b, :].rearrange("p (h t) -> p h t", h=GH))
                last.then_inc(a_kept, 1)

            def stage_y(h):
                ve.wait_ge(o_rstd, h + 1)
                ve.wait_ge(r_done, h + 1)
                ve.wait_ge(turned, gy + h)
                for b in range(TB):
                    s = slice(h * HV, (h + 1) * HV)
                    last = nc.vector.scalar_tensor_tensor(
                        out=stage[:, b, :], in0=osb[:, b, s], scalar=ohr[:, h, b:b + 1],
                        in1=gr[:, b, s], op0=ALU.mult, op1=ALU.mult)
                last.then_inc(staged, 1)

            gy = G["gla_y"]
            jobs = {(0, 2): lambda: rstd_diagonal(0), (1, 1): narrow_T_read, (1, 2): lambda: z_read(0), (2, 1): lambda: z_read(1),
                    (2, 2): gate_u}
            slots = [(t, s) for t in range(2 * QT, 12) for s in (1, 2)]
            jobs[slots[1]] = lambda: (keep(0), running_sums())
            jobs[slots[2]] = lambda: factors(1)
            for m in range(1, len(levels) + 1):
                jobs[slots[2 + m]] = lambda m=m: (keep(m), (factors(m + 1) if m < len(levels) else None))
            first = slots.index((9, 2))
            jobs[slots[first + 1]] = lambda: stage_y(0)
            jobs[slots[first + 2]] = lambda: (turn_y(gy, 0, GAIN_O), stage_y(1))
            jobs[slots[first + 3]] = lambda: (turn_y(gy + 1, 1, GAIN_O), stage_y(2))
            jobs[slots[first + 4]] = lambda: (turn_y(gy + 2, 2, GAIN_O), stage_y(3))

            def after(t):
                if (t, 2) in jobs:
                    jobs[t, 2]()
            for t in range(2 * QT + 2 * DT):
                if t == 0:
                    for j in range(CH):
                        if j in FIRST_TURNS:
                            n = FIRST_TURNS.index(j)
                            turn_x(n, GAIN_MIX0, n)
                        if j == CH - 1:
                            narrow_split(wn, wn_hi, wn_lo, 0)
                        lo(c0, j)
                    ve.wait_ge(rows_turned, 2)
                    nc.vector.tensor_copy(gcol[:, GAIN_FFN0:], wk[:, 0, GAIN_FFN0:84]).then_inc(gains_ready, 1)
                    ve.wait_ge(gains_ready, 2)
                else:
                    tile(c0, t * CH, lambda: after(t - 1),
                         (lambda: gla_qk_turn(g0 + t - 1)) if t <= 2 * QT else None, jobs.get((t, 1)))
            out_and_ffn(C["gla_o"], G["gla_o"], C["ffn0"], G["ffn0"], C["down0"], G["down0"], 4, 1,
                        lambda: after(2 * QT + 2 * DT - 1), lambda: turn_y(gy + 3, 3, GAIN_O), 0)

            cf = C["fox_in"]
            gq = G["fox_qk"]

            def head_squares(t):
                wait(ve, raw_qk, t + 1)
                nc.vector.tensor_tensor(act[:, :, :], stage[:, :, :], stage[:, :, :], ALU.mult).then_inc(head_sq, 1)
                wait(ve, head_sq, t + 1)
                wait(ve, head_rstd, t)
                nc.vector.tensor_reduce(hsum[:, :], act[:, :, :].rearrange("p b (h d) -> p (b h) d", d=HD), AX.X,
                                        ALU.add).then_inc(head_sum, 1)

            def head_norm(t):
                wait(ve, head_rstd, t + 1)
                s3 = stage[:, :, :].rearrange("p b (h d) -> p (b h) d", d=HD)
                r3 = hrstd[:, :].unsqueeze(2).to_broadcast([P, TB * 4, HD])
                nc.vector.tensor_tensor(s3, s3, r3, ALU.mult).then_inc(staged, 1)

            def fox_turn(t):
                wait(ve, turned, t + (gq + 1))
                if t.reg is None:
                    dst = fqk[:, 4 * t.base + 2:4 * t.base + 4, :]
                    gain = gcol[:, GAIN_QK + t.base:GAIN_QK + t.base + 1]
                else:
                    dst, gain = fqk[:, bass.ds(t.v * 4 + 2, 2), :], gcol[:, bass.ds(t.v + GAIN_QK, 1)]
                nc.vector.tensor_scalar(dst, tp[:, 2:4, :], gain, None, ALU.mult).then_inc(tp_lo, 1)

            tile(Lin(cf), 0, lambda: add_x(G["down0"] + 3, 11, 1, C["down0"] + DT * HCH, 3, 7),
                 lambda: turn_x(G["down0"] + 3, GAIN_MIX1, 3))
            ve.wait_ge(squared, 12)
            ve.wait_ge(x_saved, 8)
            tile(Lin(cf), CH, lambda: head_squares(Lin(0)), lambda: fox_turn(Lin(0)), late=lambda: head_norm(Lin(0)))
            tile(Lin(cf), 2 * CH, lambda: head_squares(Lin(1)), lambda: fox_turn(Lin(1)),
                 late=lambda: head_norm(Lin(1)))
            with ve.Fori(1, DT - 1) as i:
                for t in range(2):
                    tile(Lin(cf + CH, 2 * CH, i), t * CH, lambda: head_squares(Lin(t, 2, i)),
                         lambda: fox_turn(Lin(t, 2, i)), late=lambda: head_norm(Lin(t, 2, i)))
            tile(Lin(cf), 7 * CH, lambda: head_squares(Lin(6)), lambda: fox_turn(Lin(6)),
                 late=lambda: head_norm(Lin(6)))
            narrow_split(fwn, fwn_hi, fwn_lo, 1)

            def fz_read():
                ve.wait_ge(row_done, 2)
                ve.wait_ge(narrow_out, 2)
                ve.wait_ge(small_landed, 32)
                link(nc.vector.tensor_tensor(fz[:, 1, :], narrow[:, :], wk[0:FH, 1, 0:S], ALU.mult))
                nc.vector.tensor_scalar(fz[:, 0, :], fz[:, 1, :], b_f[:, 0:1], None, ALU.add).then_inc(narrow_T, 1)

            def minus_c():
                ve.wait_ge(la_done, 2)
                nc.vector.tensor_tensor_scan(fz[:, 1, :], ones[0:FH, 0:S], fz[:, 5, :], 0.0, ALU.mult,
                                             ALU.subtract).then_inc(c_ready, 1)

            def softmax_in(h0):
                for h in (h0, h0 + 1):
                    ve.wait_ge(qk_mm, h + 1)
                    if h == 0:
                        ve.wait_ge(bias_ready, 1)
                        ve.wait_ge(neg_made, 1)
                    else:
                        if h >= 2:
                            ve.wait_ge(prob_turned, h - 1)
                    p = prob[:, h % 2, :]
                    nc.vector.scalar_tensor_tensor(out=p[:, 0:P], in0=wk[:, h % 2, 0:P], scalar=HD ** -0.5,
                                                   in1=bias[:, h, 0:P], op0=ALU.mult,
                                                   op1=ALU.add).then_inc(dve_chain, 1)
                    chain[0] += 1
                    link(nc.vector.scalar_tensor_tensor(out=p[:, P:3 * P], in0=wk[:, h % 2, P:3 * P],
                                                        scalar=HD ** -0.5, in1=bias[:, h, :], op0=ALU.mult,
                                                        op1=ALU.add))
                    link(nc.vector.tensor_tensor(p[:, 0:P], p[:, 0:P], masks[:, 0, :], ALU.add))
                    nc.vector.tensor_reduce(pmax[:, h % 2, 0:1], p[:, 0:P], AX.X, ALU.max, negate=True)
                    nc.vector.tensor_reduce(pmax[:, h % 2, 1:2], p[:, P:3 * P], AX.X, ALU.max,
                                            negate=True).then_inc(max_done, 1)

            def reciprocals():
                ve.wait_ge(prob_done, FH)
                nc.vector.reciprocal(prec[:, :, :], psums[:, :, :]).then_inc(rec_done, 1)
                ve.wait_ge(rec_done, 1)

            def stage_fy(g):
                ve.wait_ge(pv_mm, g + 1)
                ve.wait_ge(og_done, g + 1)
                ve.wait_ge(turned, fy + g)
                for b in range(TB):
                    for hh in range(4):
                        s = slice(hh * HD, (hh + 1) * HD)
                        last = nc.vector.scalar_tensor_tensor(
                            out=stage[:, b, s], in0=wk[:, b, s], scalar=prec[:, b, 4 * g + hh:4 * g + hh + 1],
                            in1=og[:, g, b, s], op0=ALU.mult, op1=ALU.mult)
                last.then_inc(staged, 1)

            fy = G["fox_y"]
            jobs = {(0, 1): fz_read, (0, 2): minus_c}
            slots = [(t, s) for t in range(2 * DT) for s in (1, 2)]
            first = slots.index((1, 2))
            for h in range(0, FH, 2):
                jobs[slots[first + h // 2]] = lambda h=h: softmax_in(h)
            jobs[slots[first + 8]] = lambda: (reciprocals(), stage_fy(0))
            jobs[slots[first + 9]] = lambda: (turn_y(fy, 0, None), stage_fy(1))
            jobs[slots[first + 10]] = lambda: (turn_y(fy + 1, 1, None), stage_fy(2))
            jobs[slots[first + 11]] = lambda: turn_y(fy + 2, 2, None)
            jobs[2 * DT - 1, 2] = lambda: stage_fy(3)

            def after1(t):
                if (t, 2) in jobs:
                    jobs[t, 2]()
            rstd_diagonal(2)
            tile(Lin(C_FV), 0, lambda: head_squares(Lin(7)), lambda: fox_turn(Lin(7)), jobs.get((0, 1)),
                 late=lambda: head_norm(Lin(7)))
            for t in range(1, 2 * DT):
                tile(Lin(C_FV), t * CH, lambda: after1(t - 1), None, jobs.get((t, 1)))

            def last_x(t):
                ve.wait_ge(chunk_used, C["down1"] + (t + 1) * HCH)
                if t == 0:
                    ve.wait_ge(turned, G["ffn1"] + FT)
                else:
                    ve.wait_ge(out_stored, 16 * t)
                nc.vector.tensor_tensor(stage[:, :, :], acc[:, t % 2, :, :], xres[:, :, t * N:(t + 1) * N],
                                        ALU.add).then_inc(staged, 1)
            out_and_ffn(C["fox_o"], G["fox_o"], C["ffn1"], G["ffn1"], C["down1"], None, 12, 3,
                        lambda: after1(2 * DT - 1), lambda: turn_y(fy + 3, 3, None), 8)
            last_x(DT - 1)

        @block.gpsimd
        def _(po):
            chain = [0]

            def link(ins):
                ins.then_inc(pool_chain, 1)
                chain[0] += 1
                po.wait_ge(pool_chain, chain[0])

            def rsqrt(out_, v, size, tmp, done):
                w, y, t = tmp
                link(nc.gpsimd.tensor_scalar(w, v, 1.0 / size, EPS, ALU.mult, ALU.add))
                link(nc.gpsimd.tensor_tensor(y, w, nhalf[:, 0:w.shape[1]], ALU.pow))
                link(nc.gpsimd.tensor_tensor(t, y, y, ALU.mult))
                link(nc.gpsimd.tensor_tensor(t, t, w, ALU.mult))
                link(nc.gpsimd.tensor_scalar(t, t, -0.5, 1.5, ALU.mult, ALU.add))
                nc.gpsimd.tensor_tensor(out_, y, t, ALU.mult).then_inc(done, 1)

            def x_rstd(norm):
                po.wait_ge(squared, DT * (norm + 1))
                s = sumsq[:, norm, :, :]
                link(nc.gpsimd.tensor_tensor(s[:, :, 0:2], s[:, :, 0:2], s[:, :, 2:4], ALU.add))
                link(nc.gpsimd.tensor_tensor(s[:, :, 0], s[:, :, 0], s[:, :, 1], ALU.add))
                rsqrt(rstd[:, norm, :], s[:, :, 0], D, [psc[:, k, 0:TB] for k in range(3)], rstd_ready)

            def save(n, t):
                po.wait_ge(staged, n + 1 - DT)
                nc.gpsimd.tensor_copy(xres[:, :, t * N:(t + 1) * N], stage[:, :, :]).then_inc(x_saved, 1)

            link(nc.gpsimd.memset(ident[:, :], 0.0))
            nc.gpsimd.affine_select(out=ident[:, :], in_=ident[:, :], compare_op=ALU.not_equal, fill=1.0, base=0,
                                    pattern=[[-1, P]], channel_multiplier=1).then_inc(ident_made, 1)
            nc.gpsimd.memset(wn[:, KC * R:], 0.0).then_inc(pad_made, 1)
            link(nc.gpsimd.memset(nhalf[:, :], -0.5))
            nc.gpsimd.memset(ones[:, :], 1.0).then_inc(consts_made, 1)
            x_rstd(0)
            for m, h in enumerate(LEVELS):
                v = masks[:, m, :].rearrange("p (g two h) -> p g two h", two=2, h=h)
                nc.gpsimd.memset(v[:, :, 0, :], 0.0)
                link(nc.gpsimd.memset(v[:, :, 1, :], 1.0))
                r = v[:, :, 1, :]
                g_ = P // (2 * h)
                link(nc.gpsimd.affine_select(out=r, in_=r, compare_op=ALU.is_ge, fill=0.0, base=0,
                                             pattern=[[-2 * h, g_], [0, h]], channel_multiplier=1))
                last = nc.gpsimd.affine_select(out=r, in_=r, compare_op=ALU.is_ge, fill=0.0, base=h - 1,
                                               pattern=[[2 * h, g_], [0, h]], channel_multiplier=-1)
            last.then_inc(masks_made, 1)
            nc.gpsimd.memset(a0[:, :, :], 0.0).then_inc(a_zero, 1)
            nc.gpsimd.memset(a1[:, :, :], 0.0).then_inc(a_zero, 1)

            po.wait_ge(u_done, 2)
            po.wait_ge(z_min, 2)
            link(nc.gpsimd.tensor_tensor(absz[:, :, :], absz[:, :, :], bT[:, :, :], ALU.subtract))
            link(nc.gpsimd.tensor_tensor(minz[:, :, :], minz[:, :, :], absz[:, :, :], ALU.subtract))
            po.wait_ge(l_done, 1)
            nc.gpsimd.tensor_tensor(minz[:, :, :], minz[:, :, :], dec[:, :, :], ALU.subtract).then_inc(la_done, 1)
            po.wait_ge(b_done, 1)
            nc.gpsimd.tensor_tensor(dec[:, :, 0:P], bT[:, :, P - 1:P].to_broadcast([P, GF, P]), bT[:, :, 0:P],
                                    ALU.subtract).then_inc(d_done, 1)
            for m, h in enumerate(LEVELS):
                po.wait_ge(fac_done, m + 1)
                b4 = bT[:, :, :].rearrange("p f (g two h) -> p (f g) two h", two=2, h=h)
                d4 = dec[:, :, :].rearrange("p f (g two h) -> p (f g) two h", two=2, h=h)
                ref = b4[:, :, 0, h - 1:h].to_broadcast([P, GF * S // (2 * h), h])
                nc.gpsimd.tensor_tensor(d4[:, :, 0, :], ref, b4[:, :, 0, :], ALU.subtract)
                nc.gpsimd.tensor_tensor(d4[:, :, 1, :], b4[:, :, 1, :], ref, ALU.subtract).then_inc(d_done, 1)
            for h in range(GH):
                po.wait_ge(o_out, h + 1)
                rsqrt(ohr[:, h, :], hsum[:, 0:TB], HV, [psc[:, k, 0:TB] for k in range(3)], o_rstd)
            for t in range(DT):
                save(G["gla_o"] + t, t)
            x_rstd(1)
            for t in range(DT):
                save(G["down0"] + t, t)
            po.wait_ge(chunk_used, C["fox_in"])
            nc.gpsimd.memset(fwn[:, KC * R:], 0.0).then_inc(pad_made, 1)
            x_rstd(2)
            link(nc.gpsimd.memset(masks[:, 0, :], 0.0))
            nc.gpsimd.affine_select(out=masks[:, 0, :], in_=masks[:, 0, :], compare_op=ALU.is_ge, fill=NEG, base=0,
                                    pattern=[[-1, P]], channel_multiplier=1).then_inc(neg_made, 1)
            for t in range(2 * DT):
                po.wait_ge(head_sum, t + 1)
                rsqrt(hrstd[:, :], hsum[:, :], HD, [psc[:, k, :] for k in range(3)], head_rstd)
            po.wait_ge(narrow_T, 2)
            po.wait_ge(l_done, 2)
            link(nc.gpsimd.tensor_scalar(fz[:, 0, :], fz[:, 0, :], 0.0, None, ALU.min))
            link(nc.gpsimd.tensor_scalar(fz[:, 3, :], fz[:, 3, :], 1.0, None, ALU.subtract))
            link(nc.gpsimd.tensor_tensor(fz[:, 2, :], fz[:, 2, :], fz[:, 3, :], ALU.subtract))
            link(nc.gpsimd.tensor_tensor(fz[:, 0, :], fz[:, 0, :], fz[:, 4, :], ALU.subtract))
            nc.gpsimd.tensor_tensor(fz[:, 5, :], fz[:, 0, :], fz[:, 2, :], ALU.subtract).then_inc(la_done, 1)
            po.wait_ge(c_ready, 1)
            po.dma_start(c_dram, fz[:, 1, :]).then_inc(c_stored, 16)
            po.wait_ge(c_stored, 16)
            po.dma_start(bias[:, :, :], c_dram.rearrange("(a h) t -> a h t", a=1).to_broadcast([P, FH, S])).then_inc(bias_landed, 16)
            po.wait_ge(bias_landed, 16)
            last_half = bias[:, :, P:S]
            nc.gpsimd.affine_select(out=last_half, in_=last_half, compare_op=ALU.is_ge, fill=NEG, base=0,
                                    pattern=[[0, FH], [-1, P]], channel_multiplier=1).then_inc(bias_ready, 1)
            for t in range(DT):
                save(G["fox_o"] + t, t)
            x_rstd(3)
            for t in range(DT):
                po.wait_ge(staged, G["ffn1"] + FT + t + 1 - DT)
                po.dma_start(out[0, :, t * N:(t + 1) * N].rearrange("(b p) n -> p b n", p=P), stage[:, :, :]) \
                    .then_inc(out_stored, 16)
            po.wait_ge(out_stored, 16 * DT)


_INS = ['x', 'norm_mix', 'norm_ffn', 'gla_w_in', 'gla_w_g2', 'gla_b_g2', 'gla_o_gain', 'gla_w_o',
        'fox_w_in', 'fox_b_f', 'fox_q_gain', 'fox_k_gain', 'fox_w_o', 'ffn_w_gate', 'ffn_w_up', 'ffn_w_down']


def kernel(**inputs):
    import numpy as _np
    import concourse.bacc as _bacc
    from concourse import mybir as _mybir
    from concourse.bass_utils import run_bass_kernel_spmd as _run

    nc = _bacc.Bacc("TRN2", target_bir_lowering=False, num_devices=1)
    arrays, args = {}, []
    for name in _INS:
        a = _np.ascontiguousarray(inputs[name])
        arrays[f"in_{name}_dram"] = a
        args.append(nc.dram_tensor(f"in_{name}_dram", a.shape, _mybir.dt.from_np(a.dtype), kind="ExternalInput").ap())
    args.append(nc.dram_tensor("out_0_dram", inputs["x"].shape, _mybir.dt.float32, kind="ExternalOutput").ap())
    build(nc, *args)
    r = _run(nc, [arrays], core_ids=[0])
    return r.results[0]["out_0_dram"]
```
